# Optimizing a Trainium2 kernel written in Bass

```python
import math
import jax, jax.numpy as jnp
from jax import lax
import numpy as np

D_MODEL = 2048
BATCH = 1
SEQ = 256
DEPTH = 2

HEAD_DIM = 128
N_ATTN_HEADS = D_MODEL // (2 * HEAD_DIM)
N_CONV_GROUPS = D_MODEL // (2 * HEAD_DIM)
D_ATTN = N_ATTN_HEADS * HEAD_DIM
D_CONV = N_CONV_GROUPS * HEAD_DIM
D_MIX = D_ATTN + D_CONV
D_IN = 3 * D_ATTN + 3 * D_CONV
SPLIT_POINTS = (D_ATTN, 2 * D_ATTN, 3 * D_ATTN, 3 * D_ATTN + D_CONV, 3 * D_ATTN + 2 * D_CONV)
D_FF = 4 * D_MODEL
CONV_WIDTH = 3
DILATED_CONFIGS = ((128, 1), (512, 4), (2048, 16))
BAND_BLOCK = 128
ROPE_THETA = 10000.0
DEEPNORM_ALPHA = (2 * DEPTH) ** 0.25
DEEPNORM_BETA = (8 * DEPTH) ** -0.25
MOD_SCALE = 0.1
LN_EPS = 1e-5
RMS_EPS = 1e-6
NEG_INF = -1e30

kernel_name = "hymba_dilated_attn_shortconv_deepnorm_adaln"

def _layer_norm(x, g, b):
    xf = x.astype(jnp.float32)
    mu = jnp.mean(xf, axis=-1, keepdims=True)
    var = jnp.mean(jnp.square(xf - mu), axis=-1, keepdims=True)
    y = (xf - mu) * lax.rsqrt(var + LN_EPS) * g.astype(jnp.float32) + b.astype(jnp.float32)
    return y.astype(x.dtype)

def _group_rms_norm(x, g):
    b, s, d = x.shape
    xf = x.astype(jnp.float32).reshape(b, s, d // HEAD_DIM, HEAD_DIM)
    xf = xf * lax.rsqrt(jnp.mean(jnp.square(xf), axis=-1, keepdims=True) + RMS_EPS)
    return (xf.reshape(b, s, d) * g.astype(jnp.float32)).astype(x.dtype)

def _rotary(t):
    s, dh = t.shape[2], t.shape[3]
    inv_freq = ROPE_THETA ** (-jnp.arange(0, dh, 2, dtype=jnp.float32) / dh)
    ang = jnp.arange(s, dtype=jnp.float32)[:, None] * inv_freq[None, :]
    cos = jnp.concatenate([jnp.cos(ang), jnp.cos(ang)], axis=-1)
    sin = jnp.concatenate([jnp.sin(ang), jnp.sin(ang)], axis=-1)
    tf = t.astype(jnp.float32)
    t1, t2 = jnp.split(tf, 2, axis=-1)
    rot = jnp.concatenate([-t2, t1], axis=-1)
    return (tf * cos + rot * sin).astype(t.dtype)

def _dilated_branch(q, k, v, window, dilation):
    b, h, s, dh = q.shape
    span = window // dilation
    seg = s // dilation
    nblk = -(-seg // BAND_BLOCK)
    pad = nblk * BAND_BLOCK - seg

    def to_blocks(t):
        t = t.reshape(b, h, seg, dilation, dh).transpose(0, 1, 3, 2, 4)
        t = jnp.pad(t, ((0, 0), (0, 0), (0, 0), (0, pad), (0, 0)))
        return t.reshape(b, h, dilation, nblk, BAND_BLOCK, dh)

    def with_prev(t):
        prev = jnp.pad(t[:, :, :, :-1], ((0, 0), (0, 0), (0, 0), (1, 0), (0, 0), (0, 0)))
        return jnp.concatenate([prev, t], axis=4)

    qb = to_blocks(q)
    kk = with_prev(to_blocks(k))
    vv = with_prev(to_blocks(v))
    scores = jnp.einsum('bhrnqd,bhrnkd->bhrnqk', qb, kk,
                        preferred_element_type=jnp.float32) * (dh ** -0.5)
    qi = jnp.arange(BAND_BLOCK)[:, None]
    kj = jnp.arange(2 * BAND_BLOCK)[None, :]
    dist = BAND_BLOCK + qi - kj
    band = (dist >= 0) & (dist <= span)
    has_prev = (jnp.arange(nblk)[:, None, None] > 0) | (kj[None] >= BAND_BLOCK)
    valid = band[None] & has_prev
    scores = jnp.where(valid, scores, NEG_INF)
    lse = jax.nn.logsumexp(scores, axis=-1)
    probs = jnp.exp(scores - lse[..., None])
    out = jnp.einsum('bhrnqk,bhrnkd->bhrnqd', probs, vv.astype(jnp.float32))
    out = out.reshape(b, h, dilation, nblk * BAND_BLOCK, dh)[:, :, :, :seg]
    out = out.transpose(0, 1, 3, 2, 4).reshape(b, h, s, dh)
    lse = lse.reshape(b, h, dilation, nblk * BAND_BLOCK)[..., :seg]
    lse = lse.transpose(0, 1, 3, 2).reshape(b, h, s)
    return out, lse

def _dilated_mixture(q, k, v):
    outs, lses = [], []
    for window, dilation in DILATED_CONFIGS:
        o, l = _dilated_branch(q, k, v, window, dilation)
        outs.append(o)
        lses.append(l)
    weights = jax.nn.softmax(jnp.stack(lses, axis=0), axis=0)
    return jnp.sum(weights[..., None] * jnp.stack(outs, axis=0), axis=0)

def _causal_short_conv(h, w):
    s = h.shape[1]
    hp = jnp.pad(h, ((0, 0), (CONV_WIDTH - 1, 0), (0, 0)))
    return sum(w[i] * hp[:, i:i + s] for i in range(CONV_WIDTH))

def setup_inputs(seed: int = 0) -> dict:
    key = jax.random.key(seed)
    ks = jax.random.split(key, 16)
    f32 = jnp.float32
    col_scale = jnp.ones((D_IN,), f32).at[2 * D_ATTN:3 * D_ATTN].set(DEEPNORM_BETA)
    return {
        "x": jax.random.normal(ks[0], (BATCH, SEQ, D_MODEL), f32),
        "c": jax.random.normal(ks[1], (BATCH, D_MODEL), f32),
        "w_in": jax.random.normal(ks[2], (DEPTH, D_MODEL, D_IN), f32) * (D_MODEL ** -0.5) * col_scale,
        "conv_w": jax.random.normal(ks[3], (DEPTH, CONV_WIDTH, D_CONV), f32) * (CONV_WIDTH ** -0.5),
        "mix_norm_g": 1.0 + 0.02 * jax.random.normal(ks[4], (DEPTH, D_MIX), f32),
        "w_out": jax.random.normal(ks[5], (DEPTH, D_MIX, D_MODEL), f32) * (D_MIX ** -0.5) * DEEPNORM_BETA,
        "w_mod": jax.random.normal(ks[6], (DEPTH, D_MODEL, 6 * D_MODEL), f32) * (D_MODEL ** -0.5) * MOD_SCALE,
        "b_mod": 0.01 * jax.random.normal(ks[7], (DEPTH, 6 * D_MODEL), f32),
        "ln1_g": 1.0 + 0.02 * jax.random.normal(ks[8], (DEPTH, D_MODEL), f32),
        "ln1_b": 0.01 * jax.random.normal(ks[9], (DEPTH, D_MODEL), f32),
        "w_ff1": jax.random.normal(ks[10], (DEPTH, D_MODEL, D_FF), f32) * (D_MODEL ** -0.5) * DEEPNORM_BETA,
        "w_ff2": jax.random.normal(ks[11], (DEPTH, D_FF, D_MODEL), f32) * (D_FF ** -0.5) * DEEPNORM_BETA,
        "ln2_g": 1.0 + 0.02 * jax.random.normal(ks[12], (DEPTH, D_MODEL), f32),
        "ln2_b": 0.01 * jax.random.normal(ks[13], (DEPTH, D_MODEL), f32),
    }

def reference(x, c, w_in, conv_w, mix_norm_g, w_out, w_mod, b_mod,
              ln1_g, ln1_b, w_ff1, w_ff2, ln2_g, ln2_b):
    b, s, _ = x.shape
    cond = jax.nn.silu(c)

    def heads(t):
        return t.reshape(b, s, N_ATTN_HEADS, HEAD_DIM).transpose(0, 2, 1, 3)

    for l in range(DEPTH):
        mod = cond @ w_mod[l] + b_mod[l]
        sh1, sc1, g1, sh2, sc2, g2 = jnp.split(mod[:, None, :], 6, axis=-1)

        u = x * (1.0 + sc1) + sh1
        proj = u @ w_in[l]
        q, k, v, gate_b, gate_c, h_in = jnp.split(proj, SPLIT_POINTS, axis=-1)
        attn = _dilated_mixture(_rotary(heads(q)), _rotary(heads(k)), heads(v))
        attn = attn.transpose(0, 2, 1, 3).reshape(b, s, D_ATTN).astype(x.dtype)
        conv = gate_b * _causal_short_conv(gate_c * h_in, conv_w[l])
        mixed = _group_rms_norm(jnp.concatenate([attn, conv], axis=-1), mix_norm_g[l])
        x = _layer_norm(DEEPNORM_ALPHA * x + (1.0 + g1) * (mixed @ w_out[l]), ln1_g[l], ln1_b[l])

        u = x * (1.0 + sc2) + sh2
        ff = jnp.square(jax.nn.relu(u @ w_ff1[l])) @ w_ff2[l]
        x = _layer_norm(DEEPNORM_ALPHA * x + (1.0 + g2) * ff, ln2_g[l], ln2_b[l])
    return x


_drawn_inputs = setup_inputs


def setup_inputs(seed=0):
    import zlib

    import numpy as np

    out = dict(_drawn_inputs(seed))
    spreads = {}
    factors = {'mix_norm_g': 5.493, 'ln1_b': 3.199, 'ln2_b': 3.284}
    for name, (base, spread) in spreads.items():
        noise = np.random.default_rng([zlib.crc32(name.encode()), seed]).standard_normal(out[name].shape)
        drawn = base * np.exp(spread * noise) if base else spread * noise
        out[name] = __import__('jax').numpy.asarray(drawn.astype(out[name].dtype))
    for name, factor in factors.items():
        out[name] = (out[name] * factor).astype(out[name].dtype)
    return out
```

```python
from contextlib import ExitStack

import numpy as np
import concourse.bass as bass
from concourse import mybir

F32 = mybir.dt.float32
F32R = mybir.dt.float32r
ALU = mybir.AluOpType
ACT = mybir.ActivationFunctionType
AX_X = mybir.AxisListType.X

P = 128
D = 2048
SEQ = 256
T = SEQ // P
DEPTH = 2
HEADS = 8
FF = 4 * D
LN_EPS, RMS_EPS, NEG_INF = 1e-5, 1e-6, -1e30
ALPHA = float((2 * DEPTH) ** 0.25)
SCALE = float(P) ** -0.5

KC = D // P
GK = 2
GROUPS = KC // GK
NCOL = 512
GW = GK * NCOL
AHEAD = 4
U_IN = (6 * D // 2) // NCOL
U_OUT = D // NCOL
U_MIX = U_IN + U_OUT
BLOCKS = FF // D
U_LAYER = U_MIX + 2 * BLOCKS * (D // NCOL)

SLAB = 1024
SC = SLAB // P
SLABS = DEPTH * 6 * D // SLAB
START_SLABS = 2 * D // SLAB
MIX_SLABS = 6
MIX_MOD_AT = (0, 1, 2, 4, 5, 6)
FF_MOD_AT = (1, 3, 4, 6)
SPLITS = 56
LOOP_H = (0, 2, 4, 6)
MOD_LAYER = MIX_SLABS + 8

HEAD_AT = [[20 + 24 * g + 2 * h for h in range(4)] for g in range(2)]
Q_AT = [10, 34]
K_AT = [18, 42]
O_AT = [35, 59]
Z_AT = [66, 90]
B_AT = [72, 96]
SSQ_AT = [74, 98]
R_AT = [76, 100]
RED_AT = [22, 43, 65, 86, 107]
GATE_AT = 54


def transpose_jobs():
    at, n = {}, 0

    def add(name, count):
        nonlocal n
        at[name] = n
        n += count

    for layer in range(DEPTH):
        modded = layer < DEPTH - 1
        if layer == 0:
            add("start", START_SLABS)
        add(("fill", 2 * layer), 8)
        side = []
        for g in range(2):
            side += [(Q_AT[g], "q", 2, g), (K_AT[g], "k", 2, g), (O_AT[g], "o", 2, g)]
            side += [(HEAD_AT[g][h] + 3, "p", 1, 4 * g + h) for h in range(4)]
            side += [(Z_AT[g], "z", 2, g), (B_AT[g], "b", 2, g), (R_AT[g], "r", 2, g)]
        side += [(p, "red", 1, i) for i, p in enumerate(RED_AT)] + [(GATE_AT, "gate", 4, 0)]
        for _, name, count, i in sorted(side):
            add((name, layer, i), count)
        add(("red", layer, 5), 1)
        add(("fill", 2 * layer + 1), 8)
        add(("loop", layer), 3 * (8 + 2 * modded))
        add(("last h0", layer), 2)
        add(("last gate", layer), 4)
        add(("last h1", layer), 6)
        if modded:
            add(("last red", layer), 2)
    return at


def build(nc, x, cond_c, w_in, w_out, w_ff1, w_ff2, w_mod, b_mod, conv_w, mix_g, ln1_g, ln1_b,
          ln2_g, ln2_b, cos, sin, mask, ident, out):
    JOB = transpose_jobs()
    ctx = ExitStack()
    with ctx:
        def sb(name, shape, dt=F32):
            return ctx.enter_context(nc.sbuf_tensor(name, shape, dt))

        def sem(name):
            return ctx.enter_context(nc.semaphore(name))

        raw = sb("raw", [P, GROUPS, GW])
        w_hi = sb("w_hi", [P, AHEAD, GW], F32R)
        w_lo = sb("w_lo", [P, AHEAD, GW], F32R)
        u_hi = sb("u_hi", [P, KC, SEQ], F32R)
        u_lo = sb("u_lo", [P, KC, SEQ], F32R)
        m_hi = sb("m_hi", [P, KC, SEQ], F32R)
        m_lo = sb("m_lo", [P, KC, SEQ], F32R)
        xt = sb("xt", [P, T, D])
        gate = sb("gate", [P, D])
        mod_raw = sb("mod_raw", [P, 2, SLAB])
        mod_acc = sb("mod_acc", [P, 2, SLAB])
        Z = sb("Z", [P, 8200])
        start_raw = Z[:, 0:8 * SLAB].rearrange("p (s n) -> p s n", n=SLAB)
        utmp = Z[:, 0:1024].rearrange("p (s n) -> p s n", s=2)
        hid = Z[:, 1024:2048].rearrange("p (t n) -> p t n", t=T)
        lngb = Z[:, 2048:4096].rearrange("p (s a n) -> p s a n", s=2, a=2)
        acc = Z[:, 4096:8192].rearrange("p (t n) -> p t n", t=T)
        S = Z[:, 0:768].rearrange("p (s n) -> p s n", s=2)
        PT = Z[:, 768:1536].rearrange("p (s n) -> p s n", s=2)
        rtmp = Z[:, 1536:2048]
        A = Z[:, 2048:3072].rearrange("p (t n) -> p t n", t=T)
        B = Z[:, 3072:4096].rearrange("p (t n) -> p t n", t=T)
        V = Z[:, 4096:5120].rearrange("p (t n) -> p t n", t=T)
        KT = Z[:, 5120:6144].rearrange("p (h n) -> p h n", h=4)
        Y = KT
        ZT = Z[:, 6144:7176].rearrange("p (h n) -> p h n", h=4)
        QT = Z[:, 6144:7168].rearrange("p (h n) -> p h n", h=4)
        O = Z[:, 7176:8200].rearrange("p (t n) -> p t n", t=T)

        idn = sb("idn", [P, P])
        cs = sb("cs", [P, T, 64])
        sn = sb("sn", [P, T, 64])
        nsn = sb("nsn", [P, T, 64])
        msk = sb("msk", [P, 3 * P])
        ones = sb("ones", [P, 2])
        zero = sb("zero", [P, 1])
        junk = sb("junk", [P, T, P])
        mod_col = sb("mod_col", [P, SLABS * SC])
        mod_b = sb("mod_b", [P, SLABS * SC])
        mixg = sb("mixg", [P, DEPTH * KC])
        cw = sb("cw", [P, DEPTH * 3 * 8])
        cc_in = sb("cc_in", [P, KC])
        cc_e = sb("cc_e", [P, KC])
        cond = sb("cond", [P, KC])
        scale1 = sb("scale1", [P, KC])
        stats = sb("stats", [P, T, 4, 6])
        mv = sb("mv", [P, T, 2])
        ve = sb("ve", [P, 8])
        sd = sb("sd", [P, 8])
        rst = sb("rst", [P, 8])
        nt = sb("nt", [P, 8])
        nmu = sb("nmu", [P, T])
        mx = sb("mx", [P, 2])
        nmx = sb("nmx", [P, 2, 2])
        rsum = sb("rsum", [P, 8])
        rinv = sb("rinv", [P, 8])
        ssq = sb("ssq", [P, 8])

        banks = [ctx.enter_context(nc.psum_tensor(f"bank{i}", [P, NCOL], F32)) for i in range(8)]
        pacc = [banks[0:2], banks[2:4]]
        tb = banks[4:6]
        sbank, obank = banks[6], banks[7]

        small_in = sem("small_in")
        x_in = sem("x_in")
        raw_in = [sem(f"raw_in{j}") for j in range(GROUPS)]
        start_in = [sem(f"start_in{j}") for j in range(8)]
        mod_in = [sem(f"mod_in{j}") for j in range(2)]
        gb_in = [sem(f"gb_in{j}") for j in range(2)]
        hi_ready = sem("hi_ready")
        lo_ready = sem("lo_ready")
        pair_used = sem("pair_used")
        mod_used = sem("mod_used")
        cond_exp = sem("cond_exp")
        cond_ready = sem("cond_ready")
        ones_ready = sem("ones_ready")
        acc_read = [sem(f"acc_read{i}") for i in range(2)]
        t_done = sem("t_done")
        t_read = [sem(f"t_read{i}") for i in range(2)]
        split_hi = sem("split_hi")
        split_ready = sem("split_ready")
        s_done = sem("s_done")
        s_read = sem("s_read")
        o_done = sem("o_done")
        o_read = sem("o_read")
        max_ready = sem("max_ready")
        exp_ready = sem("exp_ready")
        rope_ready = sem("rope_ready")
        rinv_ready = sem("rinv_ready")
        o_ready = sem("o_ready")
        var_ready = sem("var_ready")
        sd_ready = sem("sd_ready")
        sq_ready = sem("sq_ready")
        rms_ready = sem("rms_ready")
        norm_ready = sem("norm_ready")
        xhat_ready = sem("xhat_ready")
        x_ready = sem("x_ready")
        hid_ready = sem("hid_ready")
        acc_zero = sem("acc_zero")
        act_step = sem("act_step")
        dve_step = sem("dve_step")
        stored = sem("stored")

        block = ctx.enter_context(nc.Block())

        def norm_index(fill):
            return 6 * ((fill - 1) // 2) + (4 if fill % 2 else 5)

        def at(b, per, const):
            return const if b is None else b * per + const

        def wait_job(eng, n):
            eng.wait_ge(t_done, n + 1)

        @block.sync
        def _(sp):
            small = [(idn[:], ident), (cs[:], cos), (sn[:], sin), (msk[:], mask), (mod_b[:], b_mod),
                     (mixg[:], mix_g), (cw[:], conv_w), (cc_in[:], cond_c)]
            for dst, src in small:
                sp.dma_start(dst, src).then_inc(small_in, 16)
            sp.dma_start(xt[:], x.rearrange("(t p) n -> p t n", p=P)).then_inc(x_in, 16)
            sp.wait_ge(mod_used, 44)

            def load(weights, row, unit, j, free=True):
                if free:
                    sp.wait_ge(lo_ready, 8 * (unit - 1) + j + 1)
                sp.dma_start(raw[:, j:j + 1, :],
                             weights[bass.ds(row, 1), :, :].rearrange("a p n -> p a n")).then_inc(raw_in[j], 16)

            for layer in range(DEPTH):
                base = U_LAYER * layer
                if layer == 0:
                    for j in range(GROUPS):
                        load(w_in, j, 0, j, free=False)
                first = 1 if layer == 0 else 0
                with sp.Fori(first, U_IN) as u:
                    for j in range(GROUPS):
                        load(w_in, (u + layer * U_IN) * GROUPS + j, u + base, j)
                with sp.Fori(0, U_OUT) as u:
                    for j in range(GROUPS):
                        load(w_out, (u + layer * U_OUT) * GROUPS + j, u + (base + U_IN), j)
                with sp.Fori(0, BLOCKS) as b:
                    for half, weights in enumerate((w_ff1, w_ff2)):
                        for u in range(4):
                            for j in range(GROUPS):
                                load(weights, (b * 4 + (layer * 4 * BLOCKS + u)) * GROUPS + j,
                                     b * 8 + (base + U_MIX + 4 * half + u), j)
            for s in range(4):
                sp.wait_ge(x_ready, 4 * (2 * DEPTH - 1) + s + 1)
                sp.dma_start(out.rearrange("(t p) n -> p t n", p=P)[:, :, s * NCOL:(s + 1) * NCOL],
                             xt[:, :, s * NCOL:(s + 1) * NCOL]).then_inc(stored, 16)
            sp.wait_ge(stored, 16 * 4)

        @block.gpsimd
        def _(pool):
            def chunk(row):
                return w_mod[bass.ds(row, 1), :, :].rearrange("a p n -> p a n")

            for k in range(8):
                pool.dma_start(start_raw[:, k:k + 1, :], chunk(k)).then_inc(start_in[k], 16)
            with pool.Fori(1, 2 * START_SLABS) as r:
                for k in range(8):
                    pool.wait_ge(mod_used, 8 * r + (k - 7))
                    pool.dma_start(start_raw[:, k:k + 1, :], chunk(r * 8 + k)).then_inc(start_in[k], 16)
            first = START_SLABS * KC
            for k in range(2):
                pool.dma_start(mod_raw[:, k:k + 1, :], chunk(first + k)).then_inc(mod_in[k], 16)
            with pool.Fori(1, (SLABS - START_SLABS) * KC // 2) as r:
                for k in range(2):
                    pool.wait_ge(mod_used, 2 * r + (first + k - 1))
                    pool.dma_start(mod_raw[:, k:k + 1, :], chunk(r * 2 + (first + k))).then_inc(mod_in[k], 16)

        @block.scalar
        def _(act):
            step = [0]

            def sync(ins):
                ins.then_inc(act_step, 1)
                step[0] += 1
                act.wait_ge(act_step, step[0])

            def prepare(unit, j, first=False):
                act.wait_ge(raw_in[j], 16 * (unit + 1))
                if not first:
                    act.wait_ge(pair_used, 8 * unit + (j - AHEAD + 1))
                nc.scalar.activation(w_hi[:, j % AHEAD, :], raw[:, j, :], ACT.Copy).then_inc(hi_ready, 1)

            def ahead(unit, j):
                prepare(unit + (j + AHEAD) // GROUPS, (j + AHEAD) % GROUPS)

            def split(n, slot, job, bank, dst, chunk, affine=None):
                wait_job(act, job)
                if affine is None:
                    act.wait_ge(split_ready, n - 1)
                    nc.scalar.activation(utmp[:, slot, :], tb[bank][:], ACT.Copy).then_inc(t_read[bank], 1)
                else:
                    if not (isinstance(n, int) and n < 2):
                        act.wait_ge(split_ready, n - 1)
                    for c in range(2):
                        scale, bias = affine(chunk + c)
                        ins = nc.scalar.activation(utmp[:, slot, c * SEQ:(c + 1) * SEQ],
                                                   tb[bank][:, c * SEQ:(c + 1) * SEQ], ACT.Identity,
                                                   bias=bias, scale=scale)
                    ins.then_inc(t_read[bank], 1)

            def split_high(read, slot, bank, dst, chunk):
                act.wait_ge(t_read[bank], read)
                nc.scalar.activation(dst[:, chunk:chunk + 2, :], utmp[:, slot, :], ACT.Copy).then_inc(split_hi, 1)

            def fill_job(fill, i):
                job = JOB[("fill", fill)] + i
                n = fill // 2 * SPLITS + fill % 2 * 16 + i
                shift = (6 * (fill // 2) + 3 * (fill % 2)) * KC
                split(n, n % 2, job, job % 2, u_hi, 2 * i,
                      lambda c: (scale1[:, c:c + 1], mod_col[:, shift + c:shift + c + 1]))
                split_high(job // 2 + 1, n % 2, job % 2, u_hi, 2 * i)

            def load_gb(fill, s):
                g, b = (ln1_g, ln1_b) if fill % 2 else (ln2_g, ln2_b)
                layer = (fill - 1) // 2
                for a, src in enumerate((g, b)):
                    act.dma_start(lngb[:, s % 2, a, :], src[layer:layer + 1, s * NCOL:(s + 1) * NCOL]
                                  .to_broadcast([P, NCOL])).then_inc(gb_in[s % 2], 16)

            def normalise(fill, s):
                if s == 0:
                    act.wait_ge(norm_ready, fill + 1)
                for t in range(T):
                    sl = xt[:, t, s * NCOL:(s + 1) * NCOL]
                    nc.scalar.activation(sl, sl, ACT.Identity, bias=nmu[:, t:t + 1],
                                         scale=rst[:, t:t + 1]).then_inc(xhat_ready, 1)

            def deviation(n):
                act.wait_ge(var_ready, n + 1)
                nc.scalar.activation(sd[:], ve[:], ACT.Sqrt).then_inc(sd_ready, 1)

            def fill_unit(fill, unit, side):
                if fill:
                    deviation(norm_index(fill))
                    normalise(fill, 0)
                    normalise(fill, 1)
                if fill == 0:
                    act.wait_ge(norm_ready, 1)
                fill_job(fill, 0)
                fill_job(fill, 1)
                if fill:
                    load_gb(fill, 2)
                    normalise(fill, 2)
                fill_job(fill, 2)
                fill_job(fill, 3)
                if fill:
                    load_gb(fill, 3)
                for j in range(GROUPS):
                    ahead(unit, j)
                    if j == 0 and fill:
                        normalise(fill, 3)
                    if j in (1, 4):
                        fill_job(fill, 4 if j == 1 else 6)
                        fill_job(fill, 5 if j == 1 else 7)
                    side(j)

            def relu_square(b, u0):
                par = u0 % 2
                act.wait_ge(pair_used, at(b, 64, 8 * u0 + 8))
                for t in range(T):
                    ins = nc.scalar.activation(hid[:, t, :], pacc[par][t][:], ACT.Relu)
                ins.then_inc(acc_read[par], 1)
                act.wait_ge(acc_read[par], at(b, 4, u0 // 2 + 1))
                nc.scalar.activation(hid[:], hid[:], ACT.Square).then_inc(hid_ready, 1)

            def mixer(layer):
                base = U_LAYER * layer

                def side(u, j):
                    p = 8 * u + j
                    for g in range(2):
                        for name, at, dst in (("q", Q_AT[g], QT), ("k", K_AT[g], KT)):
                            if p == at:
                                for i in range(2):
                                    job = JOB[(name, layer, g)] + i
                                    wait_job(act, job)
                                    nc.scalar.activation(dst[:, 2 * i:2 * i + 2, :], tb[job % 2][:],
                                                         ACT.Copy).then_inc(t_read[job % 2], 1)
                        if p == 8 * (3 * g + 2) + 7:
                            act.wait_ge(pair_used, 8 * (base + u + 1))
                            for t in range(T):
                                ins = nc.scalar.activation(V[:, t, :], pacc[u % 2][t][:], ACT.Copy)
                            ins.then_inc(acc_read[u % 2], 1)
                        for h in range(4):
                            head = 8 * layer + 4 * g + h
                            start = HEAD_AT[g][h]
                            if p == start + 1:
                                act.wait_ge(max_ready, head + 1)
                                for t in range(T):
                                    sl = S[:, h % 2, t * P:(1 + 2 * t) * P]
                                    ins = nc.scalar.activation(sl, sl, ACT.Exp, bias=nmx[:, h % 2, t:t + 1],
                                                               accum_out=rsum[:, 4 * t + h:4 * t + h + 1])
                                ins.then_inc(exp_ready, 1)
                            if p == start + 3:
                                job = JOB[("p", layer, 4 * g + h)]
                                wait_job(act, job)
                                nc.scalar.activation(PT[:, h % 2, :], tb[job % 2][:, 0:3 * P],
                                                     ACT.Copy).then_inc(t_read[job % 2], 1)
                            if p == start + 5:
                                act.wait_ge(o_done, 10 * layer + 4 * g + h + 1)
                                act.wait_ge(rinv_ready, head + 1)
                                for t in range(T):
                                    nc.scalar.activation(junk[:, t, :], obank[:, t * P:(t + 1) * P], ACT.Square,
                                                         scale=rinv[:, 4 * t + h:4 * t + h + 1],
                                                         accum_out=ssq[:, 4 * t + h:4 * t + h + 1])
                                nc.scalar.activation(O[:, :, h * P:(h + 1) * P],
                                                     obank[:, 0:T * P].rearrange("p (t n) -> p t n", t=T),
                                                     ACT.Copy).then_inc(o_read, 1)
                        if p == HEAD_AT[g][3] + 6:
                            deviation(6 * layer + g)
                        if p == O_AT[g]:
                            for i in range(2):
                                job = JOB[("o", layer, g)] + i
                                n = SPLITS * layer + 8 + 2 * g + i
                                col = KC * layer
                                split(n, n % 2, job, job % 2, m_hi, 4 * g + 2 * i,
                                      lambda c: (mixg[:, col + c:col + c + 1], 0.0))
                                split_high(job // 2 + 1, n % 2, job % 2, m_hi, 4 * g + 2 * i)
                        if p == 8 * (3 * g + 6) + 7:
                            act.wait_ge(pair_used, 8 * (base + u + 1))
                            for t in range(T):
                                ins = nc.scalar.activation(A[:, t, :], pacc[u % 2][t][:], ACT.Copy)
                            ins.then_inc(acc_read[u % 2], 1)
                        if p == Z_AT[g]:
                            for i in range(2):
                                job = JOB[("z", layer, g)] + i
                                wait_job(act, job)
                                nc.scalar.activation(ZT[:, 2 * i:2 * i + 2, 2:2 + SEQ],
                                                     tb[job % 2][:].rearrange("p (c n) -> p c n", c=2),
                                                     ACT.Copy).then_inc(t_read[job % 2], 1)
                        if p == 8 * (3 * g + 8) + 7:
                            act.wait_ge(pair_used, 8 * (base + u + 1))
                            for t in range(T):
                                ins = nc.scalar.activation(B[:, t, :], pacc[u % 2][t][:], ACT.Copy)
                            ins.then_inc(acc_read[u % 2], 1)
                        if p == B_AT[g]:
                            for i in range(2):
                                job = JOB[("b", layer, g)] + i
                                act.wait_ge(t_read[job % 2], job // 2 + 1)
                            nc.scalar.activation(ZT[:, :, 2:2 + SEQ], Y, ACT.Square).then_inc(sq_ready, 1)
                        if p == SSQ_AT[g]:
                            deviation(6 * layer + 2 + g)
                        if p == R_AT[g]:
                            for i in range(2):
                                job = JOB[("r", layer, g)] + i
                                act.wait_ge(t_read[job % 2], job // 2 + 1)
                                c = 8 + 4 * g + 2 * i
                                nc.scalar.activation(m_hi[:, c:c + 2, :], Y[:, 2 * i:2 * i + 2, :],
                                                     ACT.Copy).then_inc(split_hi, 1)
                    if p == GATE_AT:
                        gate_rows(JOB[("gate", layer, 0)])
                    if p == 8 * 13:
                        act.wait_ge(split_ready, SPLITS * layer + 16)
                        load_gb(2 * layer + 1, 0)
                        load_gb(2 * layer + 1, 1)
                    if j == 0 and u >= 14:
                        nc.scalar.activation(acc[:, u - 14, :], zero[:].to_broadcast([P, D]), ACT.Copy).then_inc(acc_zero, 1)

                for u in range(U_MIX):
                    if u == 0:
                        fill_unit(2 * layer, base, lambda j: side(0, j))
                    else:
                        for j in range(GROUPS):
                            ahead(base + u, j)
                            side(u, j)

            def gate_rows(job0):
                for i in range(4):
                    job = job0 + i
                    wait_job(act, job)
                    nc.scalar.activation(gate[:, i * NCOL:(i + 1) * NCOL], tb[job % 2][:],
                                         ACT.Identity, bias=1.0).then_inc(t_read[job % 2], 1)

            def hidden(layer, b, s, block_no, job0):
                per = 8 + 2 * (layer < DEPTH - 1)
                for i in range(2):
                    n = at(b, 8, SPLITS * layer + 24 + 8 * block_no + 2 * s + i)
                    bank = (job0 + i) % 2
                    split(n, i, at(b, per, job0 + i), bank, m_hi, 4 * s + 2 * i)
                    split_high(at(b, per // 2, (job0 + i) // 2 + 1), i, bank, m_hi, 4 * s + 2 * i)

            def mlp(layer):
                base = U_LAYER * layer + U_MIX

                def after_up(j):
                    if j == 7:
                        relu_square(None, base)

                fill_unit(2 * layer + 1, base, after_up)
                with act.Fori(0, BLOCKS - 1) as b:
                    for v in range(8):
                        for j in range(GROUPS):
                            ahead(b * 8 + (base + 1 + v), j)
                            if v < 4 and j == 2:
                                hidden(layer, b, v, 0, JOB[("loop", layer)] + LOOP_H[v])
                        if v in (0, 1, 2, 7):
                            relu_square(b, base + 1 + v)
                last = base + 8 * (BLOCKS - 1) + 1
                final = layer == DEPTH - 1
                for v in range(7):
                    for j in range(GROUPS):
                        if not (final and v == 6 and j + AHEAD >= GROUPS):
                            ahead(last + v, j)
                        if v < 4 and j == 2:
                            job0 = JOB[("last h0", layer)] if v == 0 else JOB[("last h1", layer)] + 2 * (v - 1)
                            hidden(layer, None, v, BLOCKS - 1, job0)
                        if v == 0 and j == 5:
                            gate_rows(JOB[("last gate", layer)])
                        if v == 4 and j == 0:
                            load_gb(2 * layer + 2, 0)
                            load_gb(2 * layer + 2, 1)
                    if v < 3:
                        relu_square(None, last + v)

            act.wait_ge(small_in, 16 * 8)
            act.wait_ge(ones_ready, 3)
            nc.scalar.activation(cc_e[:], cc_in[:], ACT.Exp, scale=-1.0).then_inc(cond_exp, 1)
            nc.scalar.activation(nsn[:], sn[:], ACT.Copy, scale=-1.0).then_inc(cond_exp, 1)
            for j in range(AHEAD):
                prepare(0, j, first=True)
            for layer in range(DEPTH):
                mixer(layer)
                mlp(layer)
            fill = 2 * DEPTH
            deviation(norm_index(fill))
            for s in range(4):
                normalise(fill, s)
                if s >= 1 and s < 3:
                    act.wait_ge(x_ready, 4 * (fill - 1) + s)
                    load_gb(fill, s + 1)

        @block.vector
        def _(dve):
            step = [0]

            def sync(ins):
                ins.then_inc(dve_step, 1)
                step[0] += 1
                dve.wait_ge(dve_step, step[0])

            def prepare(unit, j):
                dve.wait_ge(hi_ready, 8 * unit + (j + 1))
                nc.vector.tensor_tensor(w_lo[:, j % AHEAD, :], raw[:, j, :], w_hi[:, j % AHEAD, :].bitcast(F32),
                                        ALU.subtract).then_inc(lo_ready, 1)

            def ahead(unit, j):
                prepare(unit + (j + AHEAD) // GROUPS, (j + AHEAD) % GROUPS)

            def mod_step(n, k, par, src, arrived, count):
                dve.wait_ge(arrived, count[1])
                a = mod_acc[:, par, :]
                if k == 0:
                    ins = nc.vector.tensor_scalar(a, src, cond[:, 0:1], None, ALU.mult)
                else:
                    dve.wait_ge(mod_used, count[0])
                    ins = nc.vector.scalar_tensor_tensor(out=a, in0=src, scalar=cond[:, k:k + 1], in1=a,
                                                         op0=ALU.mult, op1=ALU.add)
                ins.then_inc(mod_used, 1)

            def mod_next(q, loop=None):
                k, par = q % KC, q // KC % 2
                first = START_SLABS * KC
                if loop is None:
                    count = (first + q, 16 * (q // 2 + 1))
                else:
                    count = (loop * 32 + (first + q), loop * 256 + 16 * (q // 2 + 1))
                mod_step(None, k, par, mod_raw[:, q % 2, :], mod_in[q % 2], count)

            def reduced(n, job, bank, loop_n=None):
                wait_job(dve, job)
                if loop_n is None:
                    cols = slice(n * SC, (n + 1) * SC)
                    o, b = mod_col[:, cols], mod_b[:, cols]
                else:
                    o, b = mod_col[:, bass.ds(loop_n, SC)], mod_b[:, bass.ds(loop_n, SC)]
                nc.vector.tensor_tensor(o, tb[bank][:, 0:SC], b, ALU.add).then_inc(t_read[bank], 1)

            def split_low(n, src, hi, lo, chunk):
                dve.wait_ge(split_hi, n + 1)
                nc.vector.tensor_tensor(lo[:, chunk:chunk + 2, :], src, hi[:, chunk:chunk + 2, :].bitcast(F32),
                                        ALU.subtract).then_inc(split_ready, 1)

            def utmp_pair(slot):
                return utmp[:, slot, :].rearrange("p (c n) -> p c n", c=2)

            def fill_low(fill, i):
                n = fill // 2 * SPLITS + fill % 2 * 16 + i
                split_low(n, utmp_pair(n % 2), u_hi, u_lo, 2 * i)

            def root(n, width, factor=None):
                dve.wait_ge(sd_ready, n + 1)
                w = slice(0, width)
                sync(nc.vector.reciprocal(rst[:, w], sd[:, w]))
                sync(nc.vector.tensor_tensor(nt[:, w], rst[:, w], rst[:, w], ALU.mult))
                sync(nc.vector.tensor_tensor(nt[:, w], nt[:, w], ve[:, w], ALU.mult))
                sync(nc.vector.tensor_scalar(nt[:, w], nt[:, w], -0.5, 1.5, ALU.mult, ALU.add))

            def statistics(fill):
                for t in range(T):
                    sync(nc.vector.bn_aggr(mv[:, t, :], stats[:, t, :, :]))
                nc.vector.tensor_scalar(ve[:, 0:T], mv[:, :, 1], LN_EPS, None, ALU.add).then_inc(var_ready, 1)
                root(norm_index(fill), T)
                sync(nc.vector.tensor_tensor(rst[:, 0:T], rst[:, 0:T], nt[:, 0:T], ALU.mult))
                if fill < 2 * DEPTH:
                    sync(plus_one(fill))
                nc.vector.scalar_tensor_tensor(out=nmu[:], in0=mv[:, :, 0], scalar=-1.0, in1=rst[:, 0:T],
                                               op0=ALU.mult, op1=ALU.mult).then_inc(norm_ready, 1)

            def plus_one(fill):
                col = (6 * (fill // 2) + 3 * (fill % 2) + 1) * KC
                return nc.vector.tensor_scalar(scale1[:], mod_col[:, col:col + KC], 1.0, None, ALU.add)

            def gain(fill, s):
                dve.wait_ge(gb_in[s % 2], 32 * (2 * (fill - 1) + s // 2 + 1))
                dve.wait_ge(xhat_ready, 8 * (fill - 1) + 2 * (s + 1))
                sl = slice(s * NCOL, (s + 1) * NCOL)
                for t in range(T):
                    ins = nc.vector.tensor_tensor(xt[:, t, sl], xt[:, t, sl], lngb[:, s % 2, 0, :], ALU.mult)
                sync(ins)
                for t in range(T):
                    ins = nc.vector.tensor_tensor(xt[:, t, sl], xt[:, t, sl], lngb[:, s % 2, 1, :], ALU.add)
                ins.then_inc(x_ready, 1)

            def fill_unit(fill, unit, side):
                if fill:
                    statistics(fill)
                    gain(fill, 0)
                    gain(fill, 1)
                fill_low(fill, 0)
                fill_low(fill, 1)
                if fill:
                    gain(fill, 2)
                fill_low(fill, 2)
                fill_low(fill, 3)
                for j in range(GROUPS):
                    ahead(unit, j)
                    if j == 0 and fill:
                        gain(fill, 3)
                    if j in (1, 4):
                        fill_low(fill, 4 if j == 1 else 6)
                        fill_low(fill, 5 if j == 1 else 7)
                    side(j)

            def residual(unit, par, s, alpha):
                dve.wait_ge(pair_used, 8 * unit + 8)
                sl = slice(s * NCOL, (s + 1) * NCOL)
                for t in range(T):
                    pr = pacc[par][t]
                    ins = nc.vector.tensor_tensor(pr[:], pr[:], gate[:, sl], ALU.mult)
                sync(ins)
                for t in range(T):
                    ins = nc.vector.scalar_tensor_tensor(out=xt[:, t, sl], in0=xt[:, t, sl], scalar=alpha,
                                                         in1=pacc[par][t][:], op0=ALU.mult, op1=ALU.add)
                ins.then_inc(acc_read[par], 1)
                dve.wait_ge(acc_read[par], unit // 2 + 1)
                for t in range(T):
                    ins = nc.vector.bn_stats(stats[:, t, s, :], xt[:, t, sl])
                sync(ins)

            def mixer(layer):
                base = U_LAYER * layer

                def side(u, j):
                    p = 8 * u + j
                    if j in MIX_MOD_AT:
                        q = 6 * u + MIX_MOD_AT.index(j)
                        mod_next(q + (layer * MOD_LAYER * KC))
                    for i, at in enumerate(RED_AT):
                        if p == at:
                            n = START_SLABS + layer * MOD_LAYER + i
                            job = JOB[("red", layer, i)]
                            reduced(n, job, job % 2)
                    for g in range(2):
                        for which in range(2):
                            if p == 8 * (3 * g + which) + 7:
                                rotate(u)
                        for h in range(4):
                            head = 8 * layer + 4 * g + h
                            start = HEAD_AT[g][h]
                            if p == start:
                                scores(head, h)
                            if p == start + 2:
                                dve.wait_ge(exp_ready, head + 1)
                                nc.vector.reciprocal(rinv[:].rearrange("p (t h) -> p t h", t=T)[:, :, h],
                                                     rsum[:].rearrange("p (t h) -> p t h", t=T)[:, :, h]
                                                     ).then_inc(rinv_ready, 1)
                        if p == HEAD_AT[g][3] + 5:
                            dve.wait_ge(o_read, 8 * layer + 4 * g + 4)
                            nc.vector.tensor_scalar(ve[:], ssq[:], 1.0 / P, RMS_EPS, ALU.mult,
                                                    ALU.add).then_inc(var_ready, 1)
                        if p == HEAD_AT[g][3] + 6:
                            root(6 * layer + g, 8)
                            sync(nc.vector.tensor_tensor(rst[:], rst[:], nt[:], ALU.mult))
                            sync(nc.vector.tensor_tensor(rst[:], rst[:], rinv[:], ALU.mult))
                            o8 = Z[:, 7176:8200].rearrange("p (i n) -> p i n", n=P)
                            nc.vector.tensor_tensor(o8, o8, rst[:].rearrange("p (i o) -> p i o", o=1).to_broadcast([P, 8, P]),
                                                    ALU.mult).then_inc(o_ready, 1)
                        if p == O_AT[g]:
                            for i in range(2):
                                n = SPLITS * layer + 8 + 2 * g + i
                                split_low(n, utmp_pair(n % 2), m_hi, m_lo, 4 * g + 2 * i)
                        if p == 8 * (3 * g + 7) + 7:
                            dve.wait_ge(pair_used, 8 * (base + u + 1))
                            dve.wait_ge(acc_read[(u - 1) % 2], (base + u - 1) // 2 + 1)
                            for t in range(T):
                                ins = nc.vector.tensor_tensor(A[:, t, :], pacc[u % 2][t][:], A[:, t, :], ALU.mult)
                            ins.then_inc(acc_read[u % 2], 1)
                            sync(nc.vector.memset(ZT[:, :, 0:2], 0.0))
                        if p == Z_AT[g] + 1:
                            convolve(layer, g)
                        if p == B_AT[g]:
                            for i in range(2):
                                job = JOB[("b", layer, g)] + i
                                wait_job(dve, job)
                                nc.vector.tensor_tensor(Y[:, 2 * i:2 * i + 2, :],
                                                        tb[job % 2][:].rearrange("p (c n) -> p c n", c=2),
                                                        Y[:, 2 * i:2 * i + 2, :], ALU.mult).then_inc(t_read[job % 2], 1)
                        if p == SSQ_AT[g]:
                            dve.wait_ge(o_done, 10 * layer + 8 + g + 1)
                            nc.vector.tensor_scalar(ve[:], obank[:, 0:8], 1.0 / P, RMS_EPS, ALU.mult,
                                                    ALU.add).then_inc(var_ready, 1)
                            root(6 * layer + 2 + g, 8)
                            nc.vector.tensor_tensor(rst[:], rst[:], nt[:], ALU.mult).then_inc(rms_ready, 1)
                        if p == R_AT[g]:
                            for i in range(2):
                                job = JOB[("r", layer, g)] + i
                                wait_job(dve, job)
                                for c in range(2):
                                    col = KC * layer + 8 + 4 * g + 2 * i + c
                                    yc = Y[:, 2 * i + c, :]
                                    ins = nc.vector.scalar_tensor_tensor(
                                        out=yc, in0=tb[job % 2][:, c * SEQ:(c + 1) * SEQ],
                                        scalar=mixg[:, col:col + 1], in1=yc, op0=ALU.mult, op1=ALU.mult)
                                ins.then_inc(t_read[job % 2], 1)
                            for i in range(2):
                                n = SPLITS * layer + 12 + 2 * g + i
                                split_low(n, Y[:, 2 * i:2 * i + 2, :], m_hi, m_lo, 8 + 4 * g + 2 * i)
                    if p == 8 * U_IN:
                        for i in (2, 3):
                            job = JOB[("gate", layer, 0)] + i
                            dve.wait_ge(t_read[job % 2], job // 2 + 1)
                    if j == 7 and u >= U_IN:
                        residual(base + u, u % 2, u - U_IN, ALPHA)

                def rotate(u):
                    dve.wait_ge(pair_used, 8 * (base + u + 1))
                    for t in range(T):
                        ps = pacc[u % 2][t][:].rearrange("p (h a n) -> p h a n", h=4, a=2)
                        o = A[:, t, :].rearrange("p (h a n) -> p h a n", h=4, a=2)
                        r = rtmp.rearrange("p (h a n) -> p h a n", h=4, a=2)

                        def rows(table):
                            return table[:, t:t + 1, :].to_broadcast([P, 4, 64])

                        for a in range(2):
                            nc.vector.tensor_tensor(o[:, :, a, :], ps[:, :, a, :], rows(cs), ALU.mult)
                        nc.vector.tensor_tensor(r[:, :, 0, :], ps[:, :, 1, :], rows(nsn), ALU.mult)
                        ins = nc.vector.tensor_tensor(r[:, :, 1, :], ps[:, :, 0, :], rows(sn), ALU.mult)
                        if t == T - 1:
                            ins.then_inc(acc_read[u % 2], 1)
                            dve.wait_ge(acc_read[u % 2], (base + u) // 2 + 1)
                        else:
                            sync(ins)
                        ins = nc.vector.tensor_tensor(A[:, t, :], A[:, t, :], rtmp, ALU.add)
                        if t == T - 1:
                            ins.then_inc(rope_ready, 1)
                        else:
                            sync(ins)

                def scores(head, h):
                    s = S[:, h % 2, :]
                    dve.wait_ge(s_done, head + 1)
                    nc.vector.scalar_tensor_tensor(out=s, in0=sbank[:, 0:3 * P], scalar=SCALE, in1=msk[:],
                                                   op0=ALU.mult, op1=ALU.add).then_inc(s_read, 1)
                    dve.wait_ge(s_read, head + 1)
                    nc.vector.tensor_reduce(mx[:, 0:1], s[:, 0:P], AX_X, ALU.max)
                    sync(nc.vector.tensor_reduce(mx[:, 1:2], s[:, P:3 * P], AX_X, ALU.max))
                    nc.vector.tensor_scalar(nmx[:, h % 2, :], mx[:], -1.0, None, ALU.mult).then_inc(max_ready, 1)

                def convolve(layer, g):
                    for i in range(2):
                        job = JOB[("z", layer, g)] + i
                        dve.wait_ge(t_read[job % 2], job // 2 + 1)
                    for tap in range(3):
                        for c in range(4):
                            col = (layer * 3 + tap) * 8 + 4 * g + c
                            w, src = cw[:, col:col + 1], ZT[:, c, tap:tap + SEQ]
                            if tap == 0:
                                ins = nc.vector.tensor_scalar(Y[:, c, :], src, w, None, ALU.mult)
                            else:
                                ins = nc.vector.scalar_tensor_tensor(out=Y[:, c, :], in0=src, scalar=w,
                                                                     in1=Y[:, c, :], op0=ALU.mult, op1=ALU.add)
                        sync(ins)

                for u in range(U_MIX):
                    if u == 0:
                        fill_unit(2 * layer, base, lambda j: side(0, j))
                    else:
                        for j in range(GROUPS):
                            ahead(base + u, j)
                            side(u, j)
                job = JOB[("red", layer, 5)]
                reduced(START_SLABS + layer * MOD_LAYER + 5, job, job % 2)

            def mlp(layer):
                base = U_LAYER * layer + U_MIX
                modded = layer < DEPTH - 1
                stride = 8 + 2 * modded
                q0 = (layer * MOD_LAYER + MIX_SLABS) * KC
                slab0 = START_SLABS + layer * MOD_LAYER + MIX_SLABS

                fill_unit(2 * layer + 1, base, lambda j: None)
                loop0 = JOB[("loop", layer)]
                with dve.Fori(0, BLOCKS - 1) as b:
                    q = 0
                    for v in range(8):
                        unit = b * 8 + (base + 1 + v)
                        for j in range(GROUPS):
                            ahead(unit, j)
                            if modded and j in FF_MOD_AT:
                                mod_next(q0 + q, loop=b)
                                q += 1
                            if v < 4 and j == 2:
                                for i in range(2):
                                    n = b * 8 + (SPLITS * layer + 24 + 2 * v + i)
                                    split_low(n, utmp_pair(i), m_hi, m_lo, 4 * v + 2 * i)
                            if modded and (v, j) in ((4, 1), (7, 7)):
                                off = 8 + (v == 7)
                                reduced(None, b * stride + (loop0 + off), (loop0 + off) % 2,
                                        loop_n=b * (2 * SC) + (slab0 + (v == 7)) * SC)
                        if 3 <= v < 7:
                            par = (v + 1) % 2
                            s = v - 3
                            sl = slice(s * NCOL, (s + 1) * NCOL)
                            dve.wait_ge(pair_used, 8 * unit + 8)
                            if v == 3:
                                dve.wait_ge(acc_zero, T * (layer + 1))
                            for t in range(T):
                                ins = nc.vector.tensor_tensor(acc[:, t, sl], pacc[par][t][:], acc[:, t, sl], ALU.add)
                            ins.then_inc(acc_read[par], 1)
                last = base + 8 * (BLOCKS - 1) + 1
                final = layer == DEPTH - 1
                q = q0 + 32 * (BLOCKS - 1)
                for v in range(7):
                    for j in range(GROUPS):
                        if not (final and v == 6 and j + AHEAD >= GROUPS):
                            ahead(last + v, j)
                        if modded and (j in FF_MOD_AT or (v < 4 and j == 7)):
                            mod_next(q)
                            q += 1
                        if v < 4 and j == 2:
                            for i in range(2):
                                n = 8 * (BLOCKS - 1) + SPLITS * layer + 24 + 2 * v + i
                                split_low(n, utmp_pair(i), m_hi, m_lo, 4 * v + 2 * i)
                        if modded and (v, j) == (4, 1):
                            job = JOB[("last red", layer)]
                            reduced(slab0 + 6, job, job % 2)
                        if v in (1, 2) and j == 5:
                            fold(layer, 2 * (v - 1))
                            fold(layer, 2 * (v - 1) + 1)
                    if v >= 3:
                        residual(last + v, (v + 1) % 2, v - 3, 1.0)
                if modded:
                    job = JOB[("last red", layer)] + 1
                    reduced(slab0 + 7, job, job % 2)

            def fold(layer, s):
                job = JOB[("last gate", layer)] + s
                dve.wait_ge(t_read[job % 2], job // 2 + 1)
                sl = slice(s * NCOL, (s + 1) * NCOL)
                par = s % 2
                if s == 0:
                    u = U_LAYER * layer + U_MIX + 8 * (BLOCKS - 1)
                    dve.wait_ge(acc_read[(u - 1) % 2], (u - 1) // 2 + 1)
                for t in range(T):
                    ins = nc.vector.tensor_tensor(acc[:, t, sl], acc[:, t, sl], gate[:, sl], ALU.mult)
                sync(ins)
                for t in range(T):
                    ins = nc.vector.scalar_tensor_tensor(out=xt[:, t, sl], in0=xt[:, t, sl], scalar=ALPHA,
                                                         in1=acc[:, t, sl], op0=ALU.mult, op1=ALU.add)
                sync(ins)

            nc.vector.memset(ones[:], 1.0).then_inc(ones_ready, 1)
            nc.vector.memset(ve[:], 1.0).then_inc(ones_ready, 1)
            nc.vector.memset(zero[:], 0.0).then_inc(ones_ready, 1)
            dve.wait_ge(small_in, 16 * 8)
            dve.wait_ge(cond_exp, 2)
            sync(nc.vector.tensor_scalar(cc_e[:], cc_e[:], 1.0, None, ALU.add))
            sync(nc.vector.reciprocal(cc_e[:], cc_e[:]))
            nc.vector.tensor_tensor(cond[:], cc_in[:], cc_e[:], ALU.mult).then_inc(cond_ready, 1)
            dve.wait_ge(cond_ready, 1)
            for n in range(START_SLABS):
                if n >= 2:
                    job = JOB["start"] + n - 2
                    reduced(n - 2, job, job % 2)
                for k in range(KC):
                    q = n * KC + k
                    mod_step(n, k, n % 2, start_raw[:, q % 8, :], start_in[q % 8], (q, 16 * (q // 8 + 1)))
            for n in range(START_SLABS - 2, START_SLABS):
                job = JOB["start"] + n
                reduced(n, job, job % 2)
            for b in range(2):
                dve.wait_ge(t_read[b], START_SLABS // 2)
            plus_one(0).then_inc(norm_ready, 1)
            for j in range(AHEAD):
                prepare(0, j)
            for layer in range(DEPTH):
                mixer(layer)
                mlp(layer)
            statistics(2 * DEPTH)
            for s in range(4):
                gain(2 * DEPTH, s)

        @block.tensor
        def _(pe):
            def begin_job(job, bank=None, reads=None):
                bank = job % 2 if bank is None else bank
                if reads is None:
                    reads = job // 2
                    if reads < 1:
                        return tb[bank]
                pe.wait_ge(t_read[bank], reads)
                return tb[bank]

            def unit_groups(b, u0, hi, lo, operand=None, side=None):
                par = u0 % 2
                unit = at(b, 8, u0)
                for j in range(GROUPS):
                    if j == 0 and u0 >= 2:
                        pe.wait_ge(acc_read[par], at(b, 4, u0 // 2))
                    if operand is not None:
                        pe.wait_ge(split_ready, operand + (j + 1))
                    pe.wait_ge(lo_ready, 8 * unit + (j + 1))
                    for kk in range(GK):
                        k = GK * j + kk
                        wh = w_hi[:, j % AHEAD, kk * NCOL:(kk + 1) * NCOL]
                        wl = w_lo[:, j % AHEAD, kk * NCOL:(kk + 1) * NCOL]
                        for t in range(T):
                            o = pacc[par][t][:]
                            tok = slice(t * P, (t + 1) * P)
                            nc.tensor.matmul(o, hi[:, k, tok], wh, start=(k == 0), stop=False)
                            nc.tensor.matmul(o, lo[:, k, tok], wh, start=False, stop=False)
                            ins = nc.tensor.matmul(o, hi[:, k, tok], wl, start=False, stop=(k == KC - 1))
                    ins.then_inc(pair_used, 1)
                    if side is not None:
                        side(j)

            def reduce_slab(par, job, bank=None, reads=None, steps=None):
                b = begin_job(job, bank, reads)
                pe.wait_ge(mod_used, steps)
                for c in range(SC):
                    ins = nc.tensor.matmul(b[:, c:c + 1], mod_acc[:, par, c * P:(c + 1) * P], ones[:, 0:1],
                                           start=True, stop=True)
                ins.then_inc(t_done, 1)

            def gate_rows(part, job0, after):
                pe.wait_ge(t_read[after % 2], after // 2 + 1)
                for i in range(4):
                    b = begin_job(job0 + i)
                    for c in range(4):
                        col = part * KC + 4 * i + c
                        ins = nc.tensor.matmul(b[:, c * P:(c + 1) * P], mod_col[:, col:col + 1].to_broadcast([P, P]),
                                               idn[:], start=True, stop=True)
                    ins.then_inc(t_done, 1)

            def turn(job, src, bank=None, reads=None):
                b = begin_job(job, bank, reads)
                for c in range(2):
                    for t in range(T):
                        ins = nc.tensor.transpose(b[:, c * SEQ + t * P:c * SEQ + (t + 1) * P], src(c, t), idn[:])
                ins.then_inc(t_done, 1)

            def fill_slice(fill, s):
                if fill:
                    pe.wait_ge(x_ready, 4 * (fill - 1) + s + 1)
                for i in range(2):
                    c0 = 4 * s + 2 * i
                    turn(JOB[("fill", fill)] + 2 * s + i,
                         lambda c, t: xt[:, t, (c0 + c) * P:(c0 + c + 1) * P])

            def fill_unit(fill, unit, side):
                fill_slice(fill, 0)
                fill_slice(fill, 1)

                def both(j):
                    if j in (1, 3):
                        fill_slice(fill, 2 if j == 1 else 3)
                    side(j)

                unit_groups(None, unit, u_hi, u_lo, operand=fill // 2 * SPLITS + fill % 2 * 16, side=both)

            def mixer(layer):
                base = U_LAYER * layer

                def side(u, j):
                    p = 8 * u + j
                    if p == GATE_AT:
                        gate_rows(6 * layer + 2, JOB[("gate", layer, 0)],
                                  JOB[("red", layer, 1)] if layer == 0 else JOB[("last red", layer - 1)] + 1)
                    for i, at in enumerate(RED_AT):
                        if p == at:
                            done = (START_SLABS + layer * MOD_LAYER + i + 1) * KC
                            reduce_slab(i % 2, JOB[("red", layer, i)], steps=done)
                    for g in range(2):
                        if p in (Q_AT[g], K_AT[g]):
                            name, which = ("q", 0) if p == Q_AT[g] else ("k", 1)
                            pe.wait_ge(rope_ready, 4 * layer + 2 * g + which + 1)
                            for i in range(2):
                                turn(JOB[(name, layer, g)] + i,
                                     lambda c, t: A[:, t, (2 * i + c) * P:(2 * i + c + 1) * P])
                        for h in range(4):
                            head = 8 * layer + 4 * g + h
                            start = HEAD_AT[g][h]
                            if p == start:
                                if h == 0:
                                    for i in range(2):
                                        job = JOB[("k", layer, g)] + i
                                        pe.wait_ge(t_read[job % 2], job // 2 + 1)
                                if head:
                                    pe.wait_ge(s_read, head)
                                nc.tensor.matmul(sbank[:, 0:P], QT[:, h, 0:P], KT[:, h, 0:P], start=True, stop=True)
                                nc.tensor.matmul(sbank[:, P:3 * P], QT[:, h, P:2 * P], KT[:, h, 0:2 * P],
                                                 start=True, stop=True).then_inc(s_done, 1)
                            if p == start + 3:
                                pe.wait_ge(exp_ready, head + 1)
                                b = begin_job(JOB[("p", layer, 4 * g + h)])
                                for i in range(3):
                                    ins = nc.tensor.transpose(b[:, i * P:(i + 1) * P],
                                                              S[:, h % 2, i * P:(i + 1) * P], idn[:])
                                ins.then_inc(t_done, 1)
                            if p == start + 5:
                                job = JOB[("p", layer, 4 * g + h)]
                                pe.wait_ge(t_read[job % 2], job // 2 + 1)
                                if h == 0:
                                    v = base + 3 * g + 2
                                    pe.wait_ge(acc_read[v % 2], v // 2 + 1)
                                if head:
                                    pe.wait_ge(o_read, head)
                                if layer and head == 8 * layer:
                                    pe.wait_ge(rms_ready, 2 * layer)
                                col = slice(h * P, (h + 1) * P)
                                nc.tensor.matmul(obank[:, 0:P], PT[:, h % 2, 0:P], V[:, 0, col], start=True, stop=True)
                                nc.tensor.matmul(obank[:, P:2 * P], PT[:, h % 2, P:2 * P], V[:, 0, col],
                                                 start=True, stop=False)
                                nc.tensor.matmul(obank[:, P:2 * P], PT[:, h % 2, 2 * P:3 * P], V[:, 1, col],
                                                 start=False, stop=True).then_inc(o_done, 1)
                        if p == O_AT[g]:
                            pe.wait_ge(o_ready, 2 * layer + g + 1)
                            for i in range(2):
                                turn(JOB[("o", layer, g)] + i,
                                     lambda c, t: O[:, t, (2 * i + c) * P:(2 * i + c + 1) * P])
                        if p == Z_AT[g]:
                            h_unit = base + 3 * g + 7
                            pe.wait_ge(acc_read[h_unit % 2], h_unit // 2 + 1)
                            for i in range(2):
                                turn(JOB[("z", layer, g)] + i,
                                     lambda c, t: A[:, t, (2 * i + c) * P:(2 * i + c + 1) * P])
                        if p == B_AT[g]:
                            b_unit = base + 3 * g + 8
                            pe.wait_ge(acc_read[b_unit % 2], b_unit // 2 + 1)
                            for i in range(2):
                                turn(JOB[("b", layer, g)] + i,
                                     lambda c, t: B[:, t, (2 * i + c) * P:(2 * i + c + 1) * P])
                        if p == SSQ_AT[g]:
                            pe.wait_ge(sq_ready, 2 * layer + g + 1)
                            if g == 0:
                                pe.wait_ge(o_read, 8 * layer + 8)
                            else:
                                pe.wait_ge(rms_ready, 2 * layer + 1)
                            for t in range(T):
                                for c in range(4):
                                    ins = nc.tensor.matmul(obank[:, 4 * t + c:4 * t + c + 1],
                                                           ZT[:, c, 2 + t * P:2 + (t + 1) * P], ones[:, 0:1],
                                                           start=True, stop=True)
                            ins.then_inc(o_done, 1)
                        if p == R_AT[g]:
                            pe.wait_ge(rms_ready, 2 * layer + g + 1)
                            for i in range(2):
                                b = begin_job(JOB[("r", layer, g)] + i)
                                for c in range(2):
                                    for t in range(T):
                                        idx = 4 * t + 2 * i + c
                                        ins = nc.tensor.matmul(b[:, c * SEQ + t * P:c * SEQ + (t + 1) * P],
                                                               rst[:, idx:idx + 1].to_broadcast([P, P]), idn[:],
                                                               start=True, stop=True)
                                ins.then_inc(t_done, 1)

                for u in range(U_MIX):
                    if u == 0:
                        fill_unit(2 * layer, base, lambda j: side(0, j))
                    elif u < U_IN:
                        unit_groups(None, base + u, u_hi, u_lo, side=lambda j: side(u, j))
                    else:
                        unit_groups(None, base + u, m_hi, m_lo, side=lambda j: side(u, j),
                                    operand=SPLITS * layer + 8 if u == U_IN else None)
                reduce_slab(1, JOB[("red", layer, 5)],
                            steps=(START_SLABS + layer * MOD_LAYER + 6) * KC)

            def mlp(layer):
                base = U_LAYER * layer + U_MIX
                modded = layer < DEPTH - 1
                stride = 8 + 2 * modded
                steps0 = (START_SLABS + layer * MOD_LAYER + MIX_SLABS) * KC
                split0 = SPLITS * layer + 24

                def turn_hidden(unit_index, job, bank=None, reads=None):
                    pe.wait_ge(hid_ready, unit_index)
                    for i in range(2):
                        turn(job + i, lambda c, t: hid[:, t, (2 * i + c) * P:(2 * i + c + 1) * P],
                             None if bank is None else (bank + i) % 2,
                             None if reads is None else reads(i))

                fill_unit(2 * layer + 1, base, lambda j: None)
                loop0 = JOB[("loop", layer)]
                with pe.Fori(0, BLOCKS - 1) as b:
                    for v in range(8):
                        def side(j, v=v):
                            if v < 4 and j == 2:
                                turn_hidden(b * 4 + (16 * layer + v + 1), b * stride + (loop0 + 2 * v),
                                            bank=(loop0 + 2 * v) % 2,
                                            reads=lambda i: b * (stride // 2) + (loop0 + 2 * v + i) // 2)
                            if modded and (v, j) in ((4, 1), (7, 7)):
                                off = 8 + (v == 7)
                                reduce_slab(int(v == 7), b * stride + (loop0 + off), bank=(loop0 + off) % 2,
                                            reads=b * (stride // 2) + (loop0 + off) // 2,
                                            steps=b * 32 + (steps0 + KC * (1 + (v == 7))))

                        up = v in (0, 1, 2, 7)
                        unit_groups(b, base + 1 + v, u_hi if up else m_hi, u_lo if up else m_lo,
                                    operand=b * 8 + split0 if v == 3 else None, side=side)
                last = base + 8 * (BLOCKS - 1) + 1
                for v in range(7):
                    def side(j, v=v):
                        if v < 4 and j == 2:
                            turn_hidden(16 * layer + 4 * (BLOCKS - 1) + v + 1,
                                        JOB[("last h0", layer)] if v == 0 else JOB[("last h1", layer)] + 2 * (v - 1))
                        if v == 0 and j == 5:
                            gate_rows(6 * layer + 5, JOB[("last gate", layer)],
                                      loop0 + 9 if modded else JOB[("red", layer, 5)])
                        if modded and (v, j) == (4, 1):
                            reduce_slab(0, JOB[("last red", layer)], steps=steps0 + 32 * (BLOCKS - 1) + KC)

                    unit_groups(None, last + v, u_hi if v < 3 else m_hi, u_lo if v < 3 else m_lo,
                                operand=split0 + 8 * (BLOCKS - 1) if v == 3 else None, side=side)
                if modded:
                    reduce_slab(1, JOB[("last red", layer)] + 1, steps=steps0 + 32 * (BLOCKS - 1) + 2 * KC)

            pe.wait_ge(ones_ready, 3)
            pe.wait_ge(small_in, 16 * 8)
            pe.wait_ge(x_in, 16)
            for n in range(START_SLABS):
                reduce_slab(n % 2, JOB["start"] + n, steps=KC * (n + 1))
            for layer in range(DEPTH):
                mixer(layer)
                mlp(layer)


def _tables():
    inv = 10000.0 ** (-np.arange(0, P, 2, dtype=np.float64) / P)
    ang = (np.arange(SEQ, dtype=np.float32)[:, None] * inv.astype(np.float32)[None, :]).astype(np.float64)
    cos = np.cos(ang).astype(np.float32).reshape(T, P, 64).transpose(1, 0, 2)
    sin = np.sin(ang).astype(np.float32).reshape(T, P, 64).transpose(1, 0, 2)
    dist = np.arange(SEQ)[:, None] - np.arange(SEQ)[None, :]
    held = np.zeros((SEQ, SEQ), np.int64)
    for window, dilation in ((128, 1), (512, 4), (2048, 16)):
        held += (dist >= 0) & (dist <= window) & (dist % dilation == 0)
    full = np.where(held > 0, np.log(np.maximum(held, 1)), NEG_INF).astype(np.float32)
    mask = np.concatenate([full[0:P, 0:P], full[P:, :]], axis=1)
    return cos, sin, mask


def _groups(w):
    n_l, k, n = w.shape
    w = w.reshape(n_l, k // D, GROUPS, GK, P, n // NCOL, NCOL)
    return np.ascontiguousarray(w.transpose(0, 1, 5, 2, 4, 3, 6)).reshape(-1, P, GW)


def kernel(x, c, w_in, conv_w, mix_norm_g, w_out, w_mod, b_mod, ln1_g, ln1_b, w_ff1, w_ff2, ln2_g, ln2_b):
    import concourse.bacc as bacc
    from concourse.bass_utils import run_bass_kernel_spmd

    cos, sin, mask = _tables()
    w_in = np.asarray(w_in)
    order = [0, 2, 4, 1, 3, 5, 8, 10, 6, 9, 11, 7]
    w_in = np.concatenate([w_in[:, :, s * NCOL:(s + 1) * NCOL] for s in order], axis=2)
    wm = np.asarray(w_mod).reshape(DEPTH, KC, P, 12 * D // 2 // SLAB, SLAB).transpose(0, 3, 1, 2, 4)
    arrays = {
        "x": np.asarray(x)[0],
        "c": np.asarray(c).reshape(KC, P).T,
        "w_in": _groups(w_in),
        "w_out": _groups(np.asarray(w_out)),
        "w_ff1": _groups(np.asarray(w_ff1)),
        "w_ff2": _groups(np.asarray(w_ff2)),
        "w_mod": wm.reshape(-1, P, SLAB),
        "b_mod": np.asarray(b_mod).reshape(SLABS * SC, P).T,
        "conv_w": np.asarray(conv_w).reshape(DEPTH * 3 * 8, P).T,
        "mix_g": np.asarray(mix_norm_g).reshape(DEPTH * KC, P).T,
        "ln1_g": np.asarray(ln1_g), "ln1_b": np.asarray(ln1_b),
        "ln2_g": np.asarray(ln2_g), "ln2_b": np.asarray(ln2_b),
        "cos": cos, "sin": sin, "mask": mask, "ident": np.eye(P, dtype=np.float32),
    }
    nc = bacc.Bacc("TRN2", target_bir_lowering=False, num_devices=1)
    args, feed = [], {}
    for name, a in arrays.items():
        a = np.ascontiguousarray(a)
        feed[f"{name}_dram"] = a
        args.append(nc.dram_tensor(f"{name}_dram", a.shape, mybir.dt.from_np(a.dtype), kind="ExternalInput").ap())
    args.append(nc.dram_tensor("out_dram", (SEQ, D), F32, kind="ExternalOutput").ap())
    build(nc, *args)
    r = run_bass_kernel_spmd(nc, [feed], core_ids=[0])
    return r.results[0]["out_dram"].reshape(1, SEQ, D)
```
